# Optimizing a Trainium2 kernel written in Bass

```python
import jax, jax.numpy as jnp
from jax import lax
import numpy as np

D_MODEL = 1024
BATCH = 1
SEQ = 4096
DEPTH = 1

HEAD_DIM = 64
SB_WIDTH = D_MODEL // 2
SB_HEADS = SB_WIDTH // HEAD_DIM
LRU_WIDTH = D_MODEL // 4
LRU_BLOCKS = LRU_WIDTH // HEAD_DIM
XA_WIDTH = D_MODEL // 4
XA_HEADS = XA_WIDTH // HEAD_DIM
D_MIX = SB_WIDTH + LRU_WIDTH + XA_WIDTH
N_MEM = 256
CONV_WIDTH = 4
LRU_C = 8.0
Q_BLOCK = 128
EPS = 1e-6
IN_SPLITS = (SB_WIDTH, SB_WIDTH, SB_WIDTH, SB_WIDTH, LRU_WIDTH, LRU_WIDTH, XA_WIDTH, XA_WIDTH)
D_IN = 4 * SB_WIDTH + 2 * LRU_WIDTH + 2 * XA_WIDTH

kernel_name = 'hymba_style_stickbreak_rglru_memxattn'

def rmsnorm(x, g):
    xf = x.astype(jnp.float32)
    y = xf * lax.rsqrt(jnp.mean(xf * xf, axis=-1, keepdims=True) + EPS)
    return (y * g.astype(jnp.float32)).astype(x.dtype)

def stick_breaking_attention(q, k, v):
    S = q.shape[2]
    scale = HEAD_DIM ** -0.5
    qf, kf, vf = q.astype(jnp.float32), k.astype(jnp.float32), v.astype(jnp.float32)
    outs = []
    for start in range(0, S, Q_BLOCK):
        end = start + Q_BLOCK
        z = jnp.einsum('bhqd,bhkd->bhqk', qf[:, :, start:end], kf[:, :, :end]) * scale
        t_idx = start + jnp.arange(Q_BLOCK)[:, None]
        s_idx = jnp.arange(end)[None, :]
        mask = s_idx < t_idx
        log_fail = jnp.where(mask, -jax.nn.softplus(z), 0.0)
        suffix = lax.cumsum(log_fail, axis=log_fail.ndim - 1, reverse=True)
        later = jnp.pad(suffix[..., 1:], ((0, 0), (0, 0), (0, 0), (0, 1)))
        w = jnp.where(mask, jnp.exp(jax.nn.log_sigmoid(z) + later), 0.0)
        outs.append(jnp.einsum('bhqk,bhkd->bhqd', w, vf[:, :, :end]))
    return jnp.concatenate(outs, axis=2).astype(v.dtype)

def causal_depthwise_conv(x, w, b):
    C = x.shape[-1]
    y = lax.conv_general_dilated(x, w[:, None, :].astype(x.dtype), window_strides=(1,),
                                 padding=[(CONV_WIDTH - 1, 0)],
                                 dimension_numbers=('NWC', 'WIO', 'NWC'),
                                 feature_group_count=C)
    return y + b.astype(x.dtype)

def rg_lru(xc, w_rg, b_rg, w_ig, b_ig, lam):
    B, S, W = xc.shape
    xf = xc.astype(jnp.float32)
    xb = xf.reshape(B, S, LRU_BLOCKS, HEAD_DIM)
    r = jax.nn.sigmoid(jnp.einsum('bsnd,nde->bsne', xb, w_rg.astype(jnp.float32)).reshape(B, S, W)
                       + b_rg.astype(jnp.float32))
    i = jax.nn.sigmoid(jnp.einsum('bsnd,nde->bsne', xb, w_ig.astype(jnp.float32)).reshape(B, S, W)
                       + b_ig.astype(jnp.float32))
    log_a = -LRU_C * r * jax.nn.softplus(-lam.astype(jnp.float32))
    a = jnp.exp(log_a)
    u = jnp.sqrt(-jnp.expm1(2.0 * log_a)) * (i * xf)

    def combine(left, right):
        a_l, b_l = left
        a_r, b_r = right
        return a_l * a_r, a_r * b_l + b_r

    _, h = lax.associative_scan(combine, (a, u), axis=1)
    return h.astype(xc.dtype)

def memory_cross_attention(xq, mem, mem_g, w_mem_kv, q_g, k_g):
    B, S, _ = xq.shape
    M = mem.shape[1]
    kv = rmsnorm(mem, mem_g) @ w_mem_kv
    mk, mv = jnp.split(kv, 2, axis=-1)
    mk = rmsnorm(mk.reshape(B, M, XA_HEADS, HEAD_DIM), k_g)
    mv = mv.reshape(B, M, XA_HEADS, HEAD_DIM)
    q = rmsnorm(xq.reshape(B, S, XA_HEADS, HEAD_DIM), q_g)
    scores = jnp.einsum('bshd,bmhd->bhsm', q.astype(jnp.float32), mk.astype(jnp.float32)) * (HEAD_DIM ** -0.5)
    p = jax.nn.softmax(scores, axis=-1)
    o = jnp.einsum('bhsm,bmhd->bshd', p, mv.astype(jnp.float32))
    return o.reshape(B, S, XA_WIDTH).astype(xq.dtype)

def hybrid_layer(x, mem, norm_g, w_in, sb_q_g, sb_k_g, conv_w, conv_b, w_rg, b_rg, w_ig, b_ig,
                 lru_lambda, xa_q_g, xa_k_g, mem_g, w_mem_kv, w_out):
    B, S, _ = x.shape
    h = rmsnorm(x, norm_g)
    proj = h @ w_in
    sb_q, sb_k, sb_v, sb_gate, lru_x, lru_gate, xa_q, xa_gate = jnp.split(
        proj, [int(c) for c in np.cumsum(IN_SPLITS)[:-1]], axis=-1)

    def to_heads(t, n):
        return t.reshape(B, S, n, HEAD_DIM).transpose(0, 2, 1, 3)

    q = rmsnorm(to_heads(sb_q, SB_HEADS), sb_q_g)
    k = rmsnorm(to_heads(sb_k, SB_HEADS), sb_k_g)
    v = to_heads(sb_v, SB_HEADS)
    sb_out = stick_breaking_attention(q, k, v).transpose(0, 2, 1, 3).reshape(B, S, SB_WIDTH)

    xc = causal_depthwise_conv(lru_x, conv_w, conv_b)
    lru_out = rg_lru(xc, w_rg, b_rg, w_ig, b_ig, lru_lambda)

    xa_out = memory_cross_attention(xa_q, mem, mem_g, w_mem_kv, xa_q_g, xa_k_g)

    y = jnp.concatenate([sb_out * jax.nn.silu(sb_gate),
                         lru_out * jax.nn.silu(lru_gate),
                         xa_out * jax.nn.silu(xa_gate)], axis=-1)
    return x + (y @ w_out).astype(x.dtype)

def setup_inputs(seed: int = 0) -> dict:
    key = jax.random.key(seed)
    ks = jax.random.split(key, 20)
    f32 = jnp.float32

    def gain(k, shape):
        return 1.0 + 0.02 * jax.random.normal(k, shape, f32)

    u = jax.random.uniform(ks[12], (DEPTH, LRU_WIDTH), f32, minval=0.9, maxval=0.999)
    a0 = u ** (1.0 / LRU_C)
    return {
        'x': jax.random.normal(ks[0], (BATCH, SEQ, D_MODEL), f32),
        'mem': jax.random.normal(ks[1], (BATCH, N_MEM, D_MODEL), f32),
        'norm_g': gain(ks[2], (DEPTH, D_MODEL)),
        'w_in': jax.random.normal(ks[3], (DEPTH, D_MODEL, D_IN), f32) * D_MODEL ** -0.5,
        'sb_q_g': gain(ks[4], (DEPTH, HEAD_DIM)),
        'sb_k_g': gain(ks[5], (DEPTH, HEAD_DIM)),
        'conv_w': jax.random.normal(ks[6], (DEPTH, CONV_WIDTH, LRU_WIDTH), f32) * CONV_WIDTH ** -0.5,
        'conv_b': 0.01 * jax.random.normal(ks[7], (DEPTH, LRU_WIDTH), f32),
        'w_rg': jax.random.normal(ks[8], (DEPTH, LRU_BLOCKS, HEAD_DIM, HEAD_DIM), f32) * HEAD_DIM ** -0.5,
        'b_rg': 0.01 * jax.random.normal(ks[9], (DEPTH, LRU_WIDTH), f32),
        'w_ig': jax.random.normal(ks[10], (DEPTH, LRU_BLOCKS, HEAD_DIM, HEAD_DIM), f32) * HEAD_DIM ** -0.5,
        'b_ig': 0.01 * jax.random.normal(ks[11], (DEPTH, LRU_WIDTH), f32),
        'lru_lambda': jnp.log(a0) - jnp.log1p(-a0),
        'xa_q_g': gain(ks[13], (DEPTH, HEAD_DIM)),
        'xa_k_g': gain(ks[14], (DEPTH, HEAD_DIM)),
        'mem_g': gain(ks[15], (DEPTH, D_MODEL)),
        'w_mem_kv': jax.random.normal(ks[16], (DEPTH, D_MODEL, 2 * XA_WIDTH), f32) * D_MODEL ** -0.5,
        'w_out': jax.random.normal(ks[17], (DEPTH, D_MIX, D_MODEL), f32) * D_MIX ** -0.5,
    }

def reference(x, mem, norm_g, w_in, sb_q_g, sb_k_g, conv_w, conv_b, w_rg, b_rg, w_ig, b_ig,
              lru_lambda, xa_q_g, xa_k_g, mem_g, w_mem_kv, w_out):
    for l in range(DEPTH):
        x = hybrid_layer(x, mem, norm_g[l], w_in[l], sb_q_g[l], sb_k_g[l], conv_w[l], conv_b[l],
                         w_rg[l], b_rg[l], w_ig[l], b_ig[l], lru_lambda[l], xa_q_g[l], xa_k_g[l],
                         mem_g[l], w_mem_kv[l], w_out[l])
    return x


_drawn_inputs = setup_inputs


def setup_inputs(seed=0):
    import zlib

    import numpy as np

    out = dict(_drawn_inputs(seed))
    spreads = {}
    factors = {'norm_g': 5.681,
     'sb_q_g': 8.0,
     'sb_k_g': 8.0,
     'conv_b': 12.635,
     'b_rg': 64.0,
     'b_ig': 64.0,
     'xa_q_g': 8.0,
     'xa_k_g': 8.0,
     'mem_g': 8.0}
    for name, (base, spread) in spreads.items():
        noise = np.random.default_rng([zlib.crc32(name.encode()), seed]).standard_normal(out[name].shape)
        drawn = base * np.exp(spread * noise) if base else spread * noise
        out[name] = __import__('jax').numpy.asarray(drawn.astype(out[name].dtype))
    for name, factor in factors.items():
        out[name] = (out[name] * factor).astype(out[name].dtype)
    return out
```

```python
from contextlib import ExitStack

import numpy as np

import concourse.bass as bass
from concourse import mybir

F32 = mybir.dt.float32
F16 = mybir.dt.float16
BF16 = mybir.dt.bfloat16
I32 = mybir.dt.int32
U32 = mybir.dt.uint32
ALU = mybir.AluOpType
ACT = mybir.ActivationFunctionType
AX = mybir.AxisListType
RMAX = bass.bass_isa.ReduceOp.max

P = 128
EPS = 1e-6
TOP = 2.0 ** 14
XTOP = 2.0 ** 10
WTOP = 2.0 ** 14
VDOWN = 2.0 ** -20
EXPONENT = 0x7F800000
LRU_C = 8.0


def hybrid_layer(nc, x, mem, norm_g, w_in, sb_q_g, sb_k_g, conv_w, conv_b, w_rg, b_rg, w_ig, b_ig,
                 lru_lambda, xa_q_g, xa_k_g, mem_g, w_mem_kv, w_out, out):
    S, D = x.shape[1], x.shape[2]
    NT = S // P
    KD = D // P
    GC = 512
    HD = sb_q_g.shape[1]
    HS = D // 2 // HD
    HX = D // 4 // HD
    NM = mem.shape[1]
    MT = NM // P
    LW = conv_w.shape[2]
    LH = LW // P
    TAPS = conv_w.shape[1]
    ZSCALE = HD ** -0.5
    HW = 2 * P
    SEG = HW + 1
    HB = HS // 2
    G_Q, G_K, G_V, G_SG, G_LRU, G_XA = range(6)
    ORDER = [G_Q, G_K, G_XA, G_LRU, G_SG, G_V]
    OC = D // GC

    x_t = x[0].rearrange("(t p) d -> t p d", p=P)
    out_t = out[0].rearrange("(t p) d -> t p d", p=P)
    w_in_g = w_in[0].rearrange("(k p) (g n) -> g p k n", p=P, n=GC)
    w_out_g = w_out[0].rearrange("(k p) (g n) -> g p k n", p=P, n=GC)
    w_kv_v = w_mem_kv[0].rearrange("(k p) n -> p k n", p=P)
    mem_v = mem[0].rearrange("(m p) d -> p m d", p=P)

    q_kept = nc.dram_tensor("q_kept", (NT, P, HS // 2, P), F32, kind="Internal").ap()
    k_kept = nc.dram_tensor("k_kept", (NT, P, HS // 2, P), F32, kind="Internal").ap()
    v_kept = nc.dram_tensor("v_kept", (NT, P, 2, GC), F16, kind="Internal").ap()
    gate_kept = nc.dram_tensor("gate_kept", (NT, P, GC), F32, kind="Internal").ap()
    carry_kept = nc.dram_tensor("carry_kept", (NT, P, HS), F32, kind="Internal").ap()

    ctx = ExitStack()
    with ctx:
        def sb(name, shape, dt=F32):
            return ctx.enter_context(nc.sbuf_tensor(name, shape, dt))

        def sem(name):
            return ctx.enter_context(nc.semaphore(name))

        w_pair = sb("w_pair", [P, 6, 2, KD, GC], F16)
        wo_pair = sb("wo_pair", [P, OC, 2, KD, GC], F16)
        fail_g = sb("fail_and_take", [P, HS * SEG + HS * HW])
        fail = fail_g[:, 0:HS * SEG].rearrange("p (h s) -> p h s", s=SEG)
        take = fail_g[:, HS * SEG:HS * SEG + HS * HW].rearrange("p (h s) -> p h s", s=HW)
        probs = fail[:, 0:HX, 0:NM]
        xy = sb("xy", [P, D])
        x_hi = sb("x_hi", [P, KD, P], F16)
        x_lo = sb("x_lo", [P, KD, P], F16)
        x_res = sb("x_res", [P, D])
        y_hi = sb("y_hi", [P, KD, P], F16)
        y_lo = sb("y_lo", [P, KD, P], F16)
        q_raw = sb("q_raw", [P, HS, HD])
        k_raw = sb("k_raw", [P, HS, HD])
        xq_raw = sb("xq_raw", [P, HX, HD])
        lx_raw = sb("lx_raw", [P, LW])
        v_sb = sb("v_sb", [P, 2, 2, GC], F16)
        k_t = sb("k_t", [P, 2, HS // 2, P])
        q_t = sb("q_t", [P, HS // 2, P])
        xq_t = sb("xq_t", [P, HX // 2, P])
        gate = sb("gate", [P, 2, D])
        turned = sb("turned", [P, 2, 2 * HB, P], F16)
        turned_f32 = turned[:, :, :, :].rearrange("p a c t -> p (a c t)").bitcast(F32).rearrange("p (c t) -> p c t", t=P)
        squares = turned[:, 0, :, :].rearrange("p c t -> p (c t)").bitcast(F32)
        mk_t = sb("mk_t", [P, HX // 2, NM])
        mv_sb = sb("mv_sb", [P, MT, HX * HD])
        conv_in = sb("conv_in", [P, LH, TAPS - 1 + P])
        xc = sb("xc", [P, LH, P])
        rec_g = sb("rec_g", [P, LH, P])
        in_g = sb("in_g", [P, LH, P])
        decay = sb("decay", [P, LH, P])
        tanh_l = sb("tanh_l", [P, LH, P])
        beta = rec_g
        h_sb = sb("h_sb", [P, LH, P])
        ident = sb("ident", [P, P])
        restart = sb("restart", [P, HB * SEG], BF16)
        rg_blocks = sb("rg_blocks", [P, LH, P])
        ig_blocks = sb("ig_blocks", [P, LH, P])
        g_in = sb("g_in", [P, KD])
        gq = sb("gq", [P, 1])
        gk = sb("gk", [P, 1])
        gxq = sb("gxq", [P, 1])
        gxk = sb("gxk", [P, 1])
        cw = sb("cw", [P, LH, TAPS])
        cb = sb("cb", [P, LH])
        brg = sb("brg", [P, LH])
        big = sb("big", [P, LH])
        lam = sb("lam", [P, LH])
        rate = sb("rate", [P, LH])
        tiny = sb("tiny", [P, 6, LH])
        mhalf_c = sb("mhalf_c", [P, 1])
        row_max = sb("row_max", [P, KD])
        w_max = sb("w_max", [P, 1])
        w_max_all = sb("w_max_all", [P, 1])
        w_exp = sb("w_exp", [P, 1])
        w_inv = sb("w_inv", [P, 1])
        g_scaled = sb("g_scaled", [P, 2, KD])
        unscale = sb("unscale", [P, 8])
        ss = sb("ss", [P, 20])
        rs = sb("rs", [P, 20])
        ss_m = sb("ss_m", [P, MT * HX])
        rs_m = sb("rs_m", [P, MT * HX])
        ss_x = sb("ss_x", [P, 1])
        rs_x = sb("rs_x", [P, 1])
        carry = sb("carry", [P, 2, HS])
        left = sb("left", [P, HS])
        left_max = sb("left_max", [P, 1])
        left_all = sb("left_all", [P, 1])
        go_on = sb("go_on", [P, 1], I32)
        mx = sb("mx", [P, HX])
        neg_mx = sb("neg_mx", [P, HX])
        den = sb("den", [P, HX])
        rden = sb("rden", [P, HX])
        y_max = sb("y_max", [P, 1])
        y_exp = sb("y_exp", [P, 1])
        y_inv = sb("y_inv", [P, 1])
        y_un = sb("y_un", [P, 2, OC])

        stage = [wo_pair[:, 0].rearrange("p a k n -> p (a k n)").bitcast(F32),
                 wo_pair[:, 1].rearrange("p a k n -> p (a k n)").bitcast(F32),
                 fail_g[:, 0:KD * GC]]
        stage = [s.rearrange("p (k n) -> p k n", n=GC) for s in stage]
        kv_raw = w_pair[:, G_V].rearrange("p a k n -> p (a k n)").bitcast(F32).rearrange("p (k n) -> p k n", n=GC)
        mem_area = w_pair[:, G_SG].rearrange("p a k n -> p (a k n)").bitcast(F32)
        mem_raw = mem_area[:, 0:MT * D].rearrange("p (m d) -> p m d", d=D)
        mem_t = mem_area[:, MT * D:2 * MT * D].rearrange("p (k m) -> p k m", m=NM)
        mem_gain = x_res[:, :]
        mk_raw = y_hi[:, :, :].rearrange("p k t -> p (k t)").bitcast(F32)
        mk_squares = y_lo[:, :, :].rearrange("p k t -> p (k t)").bitcast(F32)

        bank = [ctx.enter_context(nc.psum_tensor(f"bank{i}", [P, GC], F32)) for i in range(8)]
        PROJ = bank[0:2]
        SCORE = bank[2:4]
        TURN = bank[4:6]
        SMALL = bank[6]
        HEADS = bank[7]

        names = """turned_qk q_evac k_evac xqc_evac scores0 scores1 sig0 sig1 masked0 masked1 scan0 scan1
            w0 w1 turned_w0 turned_w1 w0_act w0_dve w1_act w1_dve heads0 heads1
            q_read k_read xa_read lru_read sg_read v_hi v_read q_sum k_sum xq_sum rs_mid rs_done normed
            gate_x gate_l gate_sb xa_scores mx_done neg_done p_done turned_p p_act p_dve
            conv gates_done gates_read tanh_done beta_steps ui_done beta_done u_done h_done
            mixed den_done rden_done gx_done y_mixed y_steps y_scaled turned_y y_hi_done y_lo_done
            x_sq x_rs_mid x_rs x_scaled turned_x x_hi_done x_lo_done out0_read out_ready left_done
            halo""".split()
        s = {n: sem("t_" + n) for n in names}
        proj_done = [sem(f"proj_done{c}") for c in range(6)]
        out_done = [sem(f"out_done{c}") for c in range(OC)]
        x_loaded = sem("x_loaded")
        res_loaded = sem("res_loaded")
        stored = sem("stored")
        kept = {k: sem(k + "_kept") for k in ("q", "k", "v", "gate", "carry")}
        const_loaded = sem("const_loaded")
        gain_loaded = sem("gain_loaded")
        mem_loaded = sem("mem_loaded")
        kv_loaded = sem("kv_loaded")
        stage_loaded = [sem(f"stage_loaded{i}") for i in range(3)]
        zeroed = sem("zeroed")
        ident_zero = sem("ident_zero")
        const_made = sem("const_made")
        w_top = sem("w_top")
        w_top_all = sem("w_top_all")
        w_factor = sem("w_factor")
        w_hi = sem("w_hi")
        w_lo = sem("w_lo")
        w_step = sem("w_step")
        lam_abs = sem("lam_abs")
        lam_exp = sem("lam_exp")
        lam_step = sem("lam_step")
        lam_done = sem("lam_done")
        fail_ones = sem("fail_ones")
        m_sq = sem("m_sq")
        m_mid = sem("m_mid")
        m_rs = sem("m_rs")
        m_scaled = sem("m_scaled")
        m_turned = sem("m_turned")
        m_evac = sem("m_evac")
        m_kv = sem("m_kv")
        m_kv_sq = sem("m_kv_sq")
        m_kv_sum = sem("m_kv_sum")
        m_kv_norm = sem("m_kv_norm")
        m_k_turned = sem("m_k_turned")
        m_done = sem("m_done")

        passed = sem("passed")
        alone = ("Pool", "SP")

        def have(eng, signal, tile, each=1, short=0, ahead_of_loop=False):
            if not isinstance(tile, int) or tile >= 0:
                eng.wait_ge(signal, each * (tile + 1) - short)
                if ahead_of_loop or (not isinstance(tile, int) and eng.engine.name in alone):
                    eng.sem_inc(passed, 1)

        def have_dma(eng, signal, tile):
            have(eng, signal, tile, 16)

        def stages(n):
            if not isinstance(n, int):
                return True, True, True, True
            return tuple(0 <= n + d < NT for d in (1, 0, -1, -2))

        def steps(eng, body):
            for n in (-1, 0, 1):
                body(n, n % 2)
            with eng.Fori(1, NT // 2 - 1) as pair:
                body(2 * pair, 0)
                body(2 * pair + 1, 1)
            for n in range(NT - 2, NT + 2):
                body(n, n % 2)

        step_names = "scored sigmoids ends scanned weights turned t_act t_dve summed added".split()
        far = {n: sem("far_" + n) for n in step_names}
        row_names = "zero gated steps scaled turned_y hi lo products result".split()
        far_row = {n: sem("far_row_" + n) for n in row_names}
        far_kv = sem("far_kv")
        far_loaded = sem("far_loaded")
        far_stored = sem("far_stored")
        left_top = sem("left_top")
        left_top_all = sem("left_top_all")
        go_on_set = sem("go_on_set")

        def rest(eng, row):
            eng.wait_ge(go_on_set, 1)
            flag = eng.value_load(go_on[0:1, 0:1])
            with eng.If(flag > 0):
                with eng.Fori(0, NT // 2 - 1) as r:
                    row(r + 2, 2 * r, (NT - 1) * r, r + 1)
                    row(NT - 1 - r, 2 * r + 1, (NT - 1) * r + r + 1, NT - 2 - r)
            eng.end_ifs()

        CH = 6 + OC
        STAGE = [0, 1, 2, 0, 1, 2, 1, 2]
        consts = [0]

        block = ctx.enter_context(nc.Block())

        @block.sync
        def _(sp):
            def load_chunk(c):
                st = STAGE[c]
                before = [b for b in range(c) if STAGE[b] == st]
                if before:
                    sp.wait_ge(w_lo, before[-1] + 1)
                src = w_in_g[ORDER[c]] if c < 6 else w_out_g[c - 6]
                sp.dma_start(stage[st], src).then_inc(stage_loaded[st], 16)

            sp.dma_start(xy[:, :], x_t[0]).then_inc(x_loaded, 16)
            sp.dma_start(g_in[:, :], norm_g[0].rearrange("(k p) -> p k", p=P), allow_slow_non_contiguous=True
                         ).then_inc(gain_loaded, 16)
            load_chunk(0)
            load_chunk(1)
            load_chunk(2)
            sp.dma_start(mem_raw, mem_v).then_inc(mem_loaded, 16)
            sp.dma_start(mem_gain, mem_g[0:1, :].to_broadcast([P, D])).then_inc(mem_loaded, 16)
            sp.dma_start(kv_raw, w_kv_v).then_inc(kv_loaded, 16)

            loads = [(cb[:, :], conv_b[0].rearrange("(h p) -> p h", p=P)),
                     (brg[:, :], b_rg[0].rearrange("(h p) -> p h", p=P)),
                     (big[:, :], b_ig[0].rearrange("(h p) -> p h", p=P)),
                     (lam[:, :], lru_lambda[0].rearrange("(h p) -> p h", p=P))]
            for h in range(LH):
                loads.append((cw[:, h, :], conv_w[0, :, h * P:(h + 1) * P].rearrange("j p -> p j")))
            for dst, src in ((gq, sb_q_g), (gk, sb_k_g), (gxq, xa_q_g), (gxk, xa_k_g)):
                for i in range(2):
                    loads.append((dst[i * HD:(i + 1) * HD, :], src[0].rearrange("(d o) -> d o", o=1)))
            for dst, src in loads:
                sp.dma_start(dst, src, allow_slow_non_contiguous=True).then_inc(const_loaded, 16)
            sp.wait_ge(zeroed, 1)
            for dst, src in ((rg_blocks, w_rg), (ig_blocks, w_ig)):
                for b in range(LW // HD):
                    r = (b % 2) * HD
                    sp.dma_start(dst[r:r + HD, b // 2, r:r + HD], src[0, b]).then_inc(const_loaded, 16)
            n_const = 16 * (len(loads) + 2 * (LW // HD))
            consts[0] = n_const

            def keep(name, dst, src, tile, ready):
                for signal in ready:
                    have(sp, signal, tile)
                sp.dma_start(dst[tile], src).then_inc(kept[name], 16)

            def body(n, p):
                X, A, B, C = stages(n)
                q = 1 - p
                if C:
                    sp.dma_start(x_res[:, :], x_t[n - 2]).then_inc(res_loaded, 16)
                if B:
                    have_dma(sp, kept["q"], n - 2)
                    have_dma(sp, kept["k"], n - 2)
                    keep("q", q_kept, q_t[:, :, :], n - 1, [s["q_evac"]])
                    keep("k", k_kept, k_t[:, q, :, :], n - 1, [s["k_evac"]])
                    have_dma(sp, kept["carry"], n - 2)
                    keep("carry", carry_kept, carry[:, q, :], n - 1, [s["w1"]])
                if X and not (isinstance(n, int) and n < 0):
                    have(sp, s["turned_y"], n - 2)
                    have(sp, s["turned_x"], n)
                    sp.dma_start(xy[:, :], x_t[n + 1]).then_inc(x_loaded, 16)
                if isinstance(n, int) and n == 0:
                    for c in range(3, CH):
                        load_chunk(c)
                if A:
                    have_dma(sp, kept["gate"], n - 1)
                    have_dma(sp, kept["v"], n - 1)
                    keep("gate", gate_kept, gate[:, p, 0:GC], n, [s["gate_sb"]])
                    keep("v", v_kept, v_sb[:, p, :, :], n, [s["v_read"]])
                if C:
                    have(sp, s["out_ready"], n - 2)
                    sp.dma_start(out_t[n - 2], x_res[:, :]).then_inc(stored, 16)
                    have_dma(sp, stored, n - 2)

            steps(sp, body)

            def row(i, w, before, n_steps):
                for dst, src in ((q_t[:, :, :], q_kept[i]), (gate[:, 0, 0:GC], gate_kept[i]),
                                 (carry[:, 0, :], carry_kept[i]), (x_res[:, :], out_t[i])):
                    sp.dma_start(dst, src).then_inc(far_loaded, 16)
                with sp.Fori(0, n_steps) as j:
                    key = nc.s_assert_within(i - 2 - j, 0, NT - 3)
                    sp.dma_start(k_t[:, 0, :, :], k_kept[key]).then_inc(far_kv, 16)
                    sp.dma_start(v_sb[:, 0, :, :], v_kept[key]).then_inc(far_kv, 16)
                    have(sp, far["summed"], before + j)
                have(sp, far_row["result"], w)
                sp.dma_start(out_t[i], x_res[:, :]).then_inc(far_stored, 16)
                have(sp, far_stored, w, 16)

            rest(sp, row)

        @block.gpsimd
        def _(pool):
            pool.memset(ident[:, :], 0.0).then_inc(ident_zero, 1)
            pool.memset(rg_blocks[:, :, :], 0.0)
            pool.memset(ig_blocks[:, :, :], 0.0).then_inc(zeroed, 1)
            pool.memset(mhalf_c[:, :], -0.5)
            pool.memset(restart[:, :], 0.0)
            pool.memset(k_t[:, 1, :, :], 0.0)
            pool.memset(v_sb[:, 1, :, :], 0.0)
            pool.memset(h_sb[:, :, :], 0.0)
            pool.memset(conv_in[:, :, :], 0.0).then_inc(zeroed, 1)
            pool.wait_ge(zeroed, 2)
            pool.memset(restart[:, :].rearrange("p (h s) -> p h s", s=SEG)[:, :, HW:SEG], 1.0)
            pool.affine_select(out=ident[:, :], in_=ident[:, :], compare_op=ALU.not_equal, fill=1.0, base=0,
                               pattern=[[-1, P]], channel_multiplier=1).then_inc(const_made, 1)

            def chunk_max(c):
                pool.wait_ge(w_top, c + 1)
                if c:
                    pool.wait_ge(w_factor, c)
                pool.partition_all_reduce(w_max_all[:, :], w_max[:, :], P, RMAX).then_inc(w_top_all, 1)

            def memory_rows():
                pool.wait_ge(m_sq, MT)
                pool.tensor_scalar(rs_m[:, 0:MT], ss_m[:, 0:MT], 1.0 / D, EPS, ALU.mult, ALU.add).then_inc(m_mid, 1)
                pool.wait_ge(m_mid, 1)
                pool.tensor_tensor(rs_m[:, 0:MT], rs_m[:, 0:MT], mhalf_c[:, :].to_broadcast([P, MT]), ALU.pow
                                   ).then_inc(m_rs, 1)

            def memory_heads():
                pool.wait_ge(m_kv_sum, MT)
                pool.tensor_scalar(rs_m[:, :], ss_m[:, :], 1.0 / HD, EPS, ALU.mult, ALU.add).then_inc(m_mid, 1)
                pool.wait_ge(m_mid, 2)
                pool.tensor_tensor(rs_m[:, :], rs_m[:, :], mhalf_c[:, :].to_broadcast([P, MT * HX]), ALU.pow
                                   ).then_inc(m_rs, 1)

            def body(n, p):
                X, A, B, C = stages(n)
                first = isinstance(n, int) and n == 0
                if first:
                    chunk_max(0)
                    memory_rows()
                    for c in range(1, 5):
                        chunk_max(c)
                    memory_heads()
                    chunk_max(5)
                if B:
                    for half in range(2):
                        have(pool, s[f"sig{half}"], n - 1)
                        hs = slice(half * HB, half * HB + HB)
                        pool.affine_select(out=fail[:, hs, P:HW], in_=fail[:, hs, P:HW], compare_op=ALU.is_gt, fill=1.0,
                                           base=0, pattern=[[0, HB], [-1, P]], channel_multiplier=1)
                        pool.affine_select(out=take[:, hs, P:HW], in_=take[:, hs, P:HW], compare_op=ALU.is_gt, fill=0.0,
                                           base=0, pattern=[[0, HB], [-1, P]], channel_multiplier=1
                                           ).then_inc(s[f"masked{half}"], 1)
                if A:
                    have(pool, s["xq_sum"], n)
                    have(pool, s["normed"], n - 1)
                    pool.tensor_scalar(rs[:, :], ss[:, :], 1.0 / HD, EPS, ALU.mult, ALU.add).then_inc(s["rs_mid"], 1)
                    have(pool, s["rs_mid"], n)
                    pool.tensor_tensor(rs[:, :], rs[:, :], mhalf_c[:, :].to_broadcast([P, 20]), ALU.pow
                                       ).then_inc(s["rs_done"], 1)
                if first:
                    chunk_max(6)
                    chunk_max(7)
                if B:
                    have(pool, s["gates_read"], n - 1)
                    have(pool, s["conv"], n - 1, TAPS)
                    pool.tensor_tensor(in_g[:, :, :], in_g[:, :, :], xc[:, :, :], ALU.mult).then_inc(s["ui_done"], 1)
                    have(pool, s["beta_done"], n - 1)
                    have(pool, s["ui_done"], n - 1)
                    pool.tensor_tensor(in_g[:, :, :], in_g[:, :, :], beta[:, :, :], ALU.mult).then_inc(s["u_done"], 1)
                if X:
                    have(pool, s["x_sq"], n + 1)
                    have(pool, s["x_scaled"], n)
                    pool.tensor_scalar(rs_x[:, :], ss_x[:, :], 1.0 / D / XTOP ** 2, EPS / XTOP ** 2, ALU.mult, ALU.add
                                       ).then_inc(s["x_rs_mid"], 1)
                    have(pool, s["x_rs_mid"], n + 1)
                    pool.tensor_tensor(rs_x[:, :], rs_x[:, :], mhalf_c[:, :], ALU.pow).then_inc(s["x_rs"], 1)
                if first:
                    pool.wait_ge(w_lo, CH)
                    pool.memset(fail[:, :, HW:SEG], 1.0).then_inc(fail_ones, 1)

            steps(pool, body)
            pool.wait_ge(left_top, 1)
            pool.partition_all_reduce(left_all[:, :], left_max[:, :], P, RMAX).then_inc(left_top_all, 1)

        @block.scalar
        def _(act):
            def memory_rows():
                act.wait_ge(mem_loaded, 32)
                for m in range(MT):
                    act.activation(mem_t[:, 0:D // NM, :].rearrange("p k m -> p (k m)"), mem_raw[:, m, :], ACT.Square,
                                   accum_out=ss_m[:, m:m + 1]).then_inc(m_sq, 1)
                    act.wait_ge(m_sq, m + 1)

            def lru_exp():
                act.wait_ge(lam_abs, 1)
                act.activation(tiny[:, 1, :], tiny[:, 0, :], ACT.Exp, scale=-1.0).then_inc(lam_exp, 1)

            def memory_values(m):
                at = slice(m * HX * HD, (m + 1) * HX * HD)
                act.wait_ge(m_kv, m + 1)
                act.activation(mv_sb[:, m, :], SCORE[m][:, HX * HD:2 * HX * HD], ACT.Copy)
                act.activation(mk_raw[:, at], SCORE[m][:, 0:HX * HD], ACT.Copy)
                act.activation(mk_squares[:, at], SCORE[m][:, 0:HX * HD], ACT.Square).then_inc(m_kv_sq, 1)

            def chunk_high(c):
                act.wait_ge(w_factor, c + 1)
                if c < 6:
                    g = ORDER[c]
                    if g in (G_SG, G_V):
                        act.wait_ge(m_kv, MT)
                    for k in range(KD):
                        last = act.activation(w_pair[:, g, 0, k, :], stage[STAGE[c]][:, k, :], ACT.Copy,
                                              scale=g_scaled[:, c % 2, k:k + 1])
                else:
                    act.wait_ge(w_lo, 4 if c == 6 else c)
                    last = act.activation(wo_pair[:, c - 6, 0], stage[STAGE[c]], ACT.Copy, scale=g_scaled[:, c % 2, 0:1])
                last.then_inc(w_hi, 1)

            def turned_high(signal):
                for b in range(2):
                    last = act.activation(turned[:, 0, 4 * b:4 * b + 4, :], TURN[b][:, :].rearrange("p (c t) -> p c t", t=P),
                                          ACT.Copy, scale=WTOP)
                last.then_inc(signal, 1)

            def body(n, p):
                X, A, B, C = stages(n)
                q = 1 - p
                first = isinstance(n, int) and n == 0
                if first:
                    chunk_high(0)
                    memory_rows()
                    chunk_high(1)
                if B:
                    have(act, s["turned_qk"], n - 1)
                    have_dma(act, kept["k"], n - 2)
                    act.activation(k_t[:, q, :, :], TURN[1][:, :].rearrange("p (c t) -> p c t", t=P), ACT.Copy,
                                   scale=gk[:, :]).then_inc(s["k_evac"], 1)
                if A:
                    have(act, proj_done[0], n)
                    have(act, s["x_sq"], n)
                    act.activation(q_raw[:, :, :], PROJ[0][:, :].rearrange("p (h d) -> p h d", d=HD), ACT.Copy,
                                   scale=unscale[:, G_Q:G_Q + 1])
                    act.activation(squares, PROJ[0][:, :], ACT.Square, scale=unscale[:, G_Q:G_Q + 1]
                                   ).then_inc(s["q_read"], 1)
                if first:
                    chunk_high(2)

                def sigmoids(half):
                    have(act, s[f"scores{half}"], n - 1)
                    for odd in range(2):
                        hs = slice(half * HB + odd, half * HB + HB, 2)
                        z = SCORE[odd][:, :].rearrange("p (h s) -> p h s", s=HW)
                        act.activation(fail[:, hs, 0:HW], z, ACT.Sigmoid, scale=-ZSCALE)
                        last = act.activation(take[:, hs, :], z, ACT.Sigmoid, scale=ZSCALE)
                    last.then_inc(s[f"sig{half}"], 1)

                if B:
                    if isinstance(n, int) and n == 1:
                        act.wait_ge(fail_ones, 1)
                    sigmoids(0)
                if A:
                    have(act, proj_done[1], n)
                    have(act, s["q_sum"], n)
                    act.activation(k_raw[:, :, :], PROJ[1][:, :].rearrange("p (h d) -> p h d", d=HD), ACT.Copy,
                                   scale=unscale[:, G_K:G_K + 1])
                    act.activation(squares, PROJ[1][:, :], ACT.Square, scale=unscale[:, G_K:G_K + 1]
                                   ).then_inc(s["k_read"], 1)
                if first:
                    chunk_high(3)
                    for m in range(MT):
                        memory_values(m)
                    lru_exp()
                    chunk_high(4)
                if B:
                    sigmoids(1)
                if A:
                    have(act, proj_done[2], n)
                    have(act, s["k_sum"], n)
                    have(act, s["y_mixed"], n - 2)
                    u = unscale[:, G_XA:G_XA + 1]
                    act.activation(xq_raw[:, :, :], PROJ[0][:, 0:HX * HD].rearrange("p (h d) -> p h d", d=HD), ACT.Copy,
                                   scale=u)
                    act.activation(squares[:, 0:HX * HD], PROJ[0][:, 0:HX * HD], ACT.Square, scale=u)
                    act.activation(gate[:, p, D - HX * HD:D], PROJ[0][:, HX * HD:GC], ACT.Sigmoid, scale=u
                                   ).then_inc(s["xa_read"], 1)
                if first:
                    chunk_high(5)
                if B:
                    have(act, s["gates_done"], n - 1)
                    have(act, s["h_done"], n - 2)
                    for g, (dst, bias) in enumerate(((rec_g, brg), (in_g, big))):
                        for h in range(LH):
                            at = (g * LH + h) * P
                            last = act.activation(dst[:, h, :], SMALL[:, at:at + P], ACT.Sigmoid, bias=bias[:, h:h + 1])
                    last.then_inc(s["gates_read"], 1)
                if C:
                    have(act, s["turned_y"], n - 2)
                    for b in range(2):
                        last = act.activation(y_hi[:, 4 * b:4 * b + 4, :], TURN[b][:, :].rearrange("p (k t) -> p k t", t=P),
                                              ACT.Copy)
                    last.then_inc(s["y_hi_done"], 1)
                if B:
                    have(act, s["gates_read"], n - 1)
                    if isinstance(n, int) and n == 1:
                        act.wait_ge(lam_done, 1)
                    for h in range(LH):
                        act.activation(tanh_l[:, h, :], rec_g[:, h, :], ACT.Tanh, scale=rate[:, h:h + 1])
                        last = act.activation(decay[:, h, :], rec_g[:, h, :], ACT.Exp, scale=rate[:, h:h + 1])
                    last.then_inc(s["tanh_done"], 1)
                    have(act, s["neg_done"], n - 1)
                    have(act, s["w0"], n - 1)
                    have(act, s["rden_done"], n - 2)
                    for h in range(HX):
                        last = act.activation(probs[:, h, :], SCORE[h % 2][:, (h // 2) * NM:(h // 2 + 1) * NM], ACT.Exp,
                                              bias=neg_mx[:, h:h + 1], scale=ZSCALE, accum_out=den[:, h:h + 1])
                    last.then_inc(s["p_done"], 1)
                if X:
                    have_dma(act, x_loaded, n + 1)
                    have(act, s["xq_sum"], n)
                    act.activation(squares.bitcast(BF16), xy[:, :], ACT.Square, accum_out=ss_x[:, :]
                                   ).then_inc(s["x_sq"], 1)
                if A:
                    have(act, proj_done[3], n)
                    u = unscale[:, G_LRU:G_LRU + 1]
                    act.activation(lx_raw[:, :], PROJ[1][:, 0:LW], ACT.Copy, scale=u)
                    act.activation(gate[:, p, D // 2:D // 2 + LW], PROJ[1][:, LW:GC], ACT.Sigmoid, scale=u
                                   ).then_inc(s["lru_read"], 1)
                if first:
                    chunk_high(6)

                def weights_high(turned_done, evac_done):
                    have(act, turned_done, n - 1)
                    have(act, s["xq_sum"], n if A else n - 1)
                    if X:
                        have(act, s["x_sq"], n + 1)
                    turned_high(evac_done)

                if B:
                    weights_high(s["turned_w0"], s["w0_act"])
                    have(act, s["beta_steps"], n - 1, 3)
                    act.activation(beta[:, :, :], beta[:, :, :], ACT.Sqrt).then_inc(s["beta_done"], 1)
                if A:
                    have(act, proj_done[4], n)
                    have_dma(act, kept["gate"], n - 1)
                    act.activation(gate[:, p, 0:GC], PROJ[0][:, :], ACT.Sigmoid, scale=unscale[:, G_SG:G_SG + 1]
                                   ).then_inc(s["sg_read"], 1)
                if B:
                    weights_high(s["turned_w1"], s["w1_act"])
                if A:
                    have(act, proj_done[5], n)
                    have(act, s["heads1"], n - 1)
                    have_dma(act, kept["v"], n - 1)
                    act.activation(v_sb[:, p, 0, :], PROJ[1][:, :], ACT.Copy, scale=VDOWN).then_inc(s["v_hi"], 1)
                if B:
                    have(act, s["turned_p"], n - 1)
                    act.activation(turned_f32[:, 0:4, :], TURN[0][:, :].rearrange("p (c t) -> p c t", t=P), ACT.Copy
                                   ).then_inc(s["p_act"], 1)
                if X:
                    have(act, s["turned_x"], n + 1)
                    for b in range(2):
                        last = act.activation(x_hi[:, 4 * b:4 * b + 4, :], TURN[b][:, :].rearrange("p (k t) -> p k t", t=P),
                                              ACT.Copy)
                    last.then_inc(s["x_hi_done"], 1)
                if first:
                    chunk_high(7)

            steps(act, body)

            def row(i, w, before, n_steps):
                with act.Fori(0, n_steps) as j:
                    u = before + j
                    have(act, far["scored"], u)
                    for odd in range(2):
                        z = SCORE[odd][:, :].rearrange("p (h s) -> p h s", s=P)
                        act.activation(fail[:, odd::2, 0:P], z, ACT.Sigmoid, scale=-ZSCALE)
                        last = act.activation(take[:, odd::2, 0:P], z, ACT.Sigmoid, scale=ZSCALE)
                    last.then_inc(far["sigmoids"], 1)
                    have(act, far["turned"], u)
                    turned_high(far["t_act"])
                    have(act, far["summed"], u)
                have(act, far_row["turned_y"], w)
                act.activation(y_hi[:, 0:4, :], TURN[0][:, :].rearrange("p (c t) -> p c t", t=P), ACT.Copy
                               ).then_inc(far_row["hi"], 1)

            rest(act, row)

        @block.vector
        def _(dve):
            def lru_start():
                dve.wait_ge(const_loaded, consts[0])
                dve.scalar_tensor_tensor(tiny[:, 0, :], lam[:, :], -1.0, lam[:, :], ALU.mult, ALU.max).then_inc(lam_abs, 1)

            def lru_rate():
                dve.wait_ge(lam_exp, 1)
                count = [0]

                def lam_next(ins):
                    count[0] += 1
                    ins.then_inc(lam_step, 1)
                    dve.wait_ge(lam_step, count[0])

                lam_next(dve.tensor_scalar(tiny[:, 2, :], tiny[:, 1, :], 2.0, None, ALU.add))
                lam_next(dve.reciprocal(tiny[:, 3, :], tiny[:, 2, :]))
                lam_next(dve.tensor_tensor(tiny[:, 2, :], tiny[:, 1, :], tiny[:, 3, :], ALU.mult))
                lam_next(dve.tensor_tensor(tiny[:, 3, :], tiny[:, 2, :], tiny[:, 2, :], ALU.mult))
                lam_next(dve.tensor_scalar(tiny[:, 4, :], tiny[:, 3, :], 1.0 / 19, 1.0 / 17, ALU.mult, ALU.add))
                for odd in (15, 13, 11, 9, 7, 5, 3, 1):
                    lam_next(dve.tensor_tensor(tiny[:, 4, :], tiny[:, 4, :], tiny[:, 3, :], ALU.mult))
                    lam_next(dve.tensor_scalar(tiny[:, 4, :], tiny[:, 4, :], 1.0 / odd, None, ALU.add))
                lam_next(dve.tensor_tensor(tiny[:, 4, :], tiny[:, 4, :], tiny[:, 2, :], ALU.mult))
                lam_next(dve.tensor_scalar(tiny[:, 5, :], lam[:, :], -1.0, 0.0, ALU.mult, ALU.max))
                lam_next(dve.scalar_tensor_tensor(rate[:, :], tiny[:, 4, :], 2.0, tiny[:, 5, :], ALU.mult, ALU.add))
                dve.tensor_scalar(rate[:, :], rate[:, :], -LRU_C, None, ALU.mult).then_inc(lam_done, 1)

            def memory_scale():
                dve.wait_ge(m_rs, 1)
                dve.wait_ge(mem_loaded, 32)
                for m in range(MT):
                    dve.scalar_tensor_tensor(mem_raw[:, m, :], mem_raw[:, m, :], rs_m[:, m:m + 1], mem_gain,
                                             ALU.mult, ALU.mult).then_inc(m_scaled, 1)

            w_count = [0]

            def w_next(ins):
                w_count[0] += 1
                ins.then_inc(w_step, 1)
                dve.wait_ge(w_step, w_count[0])

            def chunk_top(c):
                st = STAGE[c]
                dve.wait_ge(stage_loaded[st], 16 * STAGE[:c + 1].count(st))
                w_next(dve.tensor_reduce(row_max[:, :], stage[st], AX.X, ALU.max, apply_absolute_value=True))
                if c == 0:
                    dve.wait_ge(gain_loaded, 16)
                if c < 6:
                    w_next(dve.tensor_tensor(row_max[:, :], row_max[:, :], g_in[:, :], ALU.mult))
                if c:
                    dve.wait_ge(w_top_all, c)
                dve.tensor_reduce(w_max[:, :], row_max[:, :], AX.X, ALU.max, apply_absolute_value=True).then_inc(w_top, 1)

            def chunk_factor(c):
                dve.wait_ge(w_top_all, c + 1)
                w_next(dve.tensor_scalar(w_exp[:, :], w_max_all[:, :], 1e-30, None, ALU.max))
                w_next(dve.tensor_scalar(w_exp[:, :].bitcast(U32), w_exp[:, :].bitcast(U32), EXPONENT, None, ALU.bitwise_and))
                w_next(dve.reciprocal(w_inv[:, :], w_exp[:, :]))
                at = ORDER[c] if c < 6 else c
                undo = 1.0 / TOP / (XTOP if c < 6 else 1.0)
                if at == G_V:
                    undo /= VDOWN * WTOP
                dve.tensor_scalar(unscale[:, at:at + 1], w_exp[:, :], undo, None, ALU.mult)
                if c >= 2:
                    dve.wait_ge(w_hi, c - 1)
                if c < 6:
                    ins = dve.tensor_scalar(g_scaled[:, c % 2, :], g_in[:, :], w_inv[:, :], TOP, ALU.mult, ALU.mult)
                else:
                    ins = dve.tensor_scalar(g_scaled[:, c % 2, 0:1], w_inv[:, :], TOP, None, ALU.mult)
                ins.then_inc(w_factor, 1)

            def chunk_low(c):
                dve.wait_ge(w_hi, c + 1)
                dve.wait_ge(w_factor, c + 1)
                if c < 6:
                    g = ORDER[c]
                    for k in range(KD):
                        last = dve.scalar_tensor_tensor(w_pair[:, g, 1, k, :], stage[STAGE[c]][:, k, :],
                                                        g_scaled[:, c % 2, k:k + 1], w_pair[:, g, 0, k, :],
                                                        ALU.mult, ALU.subtract)
                    last.then_inc(w_lo, 1)
                else:
                    flat = "p k n -> p (k n)"
                    dve.scalar_tensor_tensor(wo_pair[:, c - 6, 1].rearrange(flat), stage[STAGE[c]].rearrange(flat),
                                             g_scaled[:, c % 2, 0:1], wo_pair[:, c - 6, 0].rearrange(flat),
                                             ALU.mult, ALU.subtract).then_inc(w_lo, 1)

            def memory_turned(m):
                dve.wait_ge(m_turned, m + 1)
                for b in range(2):
                    last = dve.tensor_copy(mem_t[:, 4 * b:4 * b + 4, m * P:(m + 1) * P],
                                           TURN[b][:, :].rearrange("p (k t) -> p k t", t=P))
                last.then_inc(m_evac, 1)

            def memory_keys():
                for m in range(MT):
                    dve.wait_ge(m_kv_sq, m + 1)
                    at = slice(m * HX * HD, (m + 1) * HX * HD)
                    dve.tensor_reduce(ss_m[:, m * HX:(m + 1) * HX], mk_squares[:, at].rearrange("p (h d) -> p h d", d=HD),
                                      AX.X, ALU.add).then_inc(m_kv_sum, 1)

            def memory_keys_norm():
                dve.wait_ge(m_rs, 2)
                heads = mk_raw.rearrange("p (h d) -> p h d", d=HD)
                dve.tensor_tensor(heads, heads, rs_m[:, :].unsqueeze(2).to_broadcast([P, MT * HX, HD]), ALU.mult
                                  ).then_inc(m_kv_norm, 1)

            def memory_keys_turned():
                dve.wait_ge(m_k_turned, 1)
                for m in range(MT):
                    last = dve.tensor_scalar(mk_t[:, :, m * P:(m + 1) * P],
                                             SMALL[:, m * 2 * P:(m + 1) * 2 * P].rearrange("p (c t) -> p c t", t=P),
                                             gxk[:, :], None, ALU.mult)
                last.then_inc(m_done, 1)

            def turned_low(signal):
                for b in range(2):
                    last = dve.scalar_tensor_tensor(turned[:, 1, 4 * b:4 * b + 4, :],
                                                    TURN[b][:, :].rearrange("p (c t) -> p c t", t=P), WTOP,
                                                    turned[:, 0, 4 * b:4 * b + 4, :], ALU.mult, ALU.subtract)
                last.then_inc(signal, 1)

            def body(n, p):
                X, A, B, C = stages(n)
                q = 1 - p
                first = isinstance(n, int) and n == 0

                def next_chunk(c):
                    chunk_factor(c)
                    chunk_top(c + 1)
                    chunk_low(c)

                if first:
                    next_chunk(0)
                    memory_scale()
                    next_chunk(1)
                if B:
                    have(dve, s["turned_qk"], n - 1)
                    have_dma(dve, kept["q"], n - 2)
                    dve.tensor_scalar(q_t[:, :, :], TURN[0][:, :].rearrange("p (c t) -> p c t", t=P), gq[:, :], None,
                                      ALU.mult).then_inc(s["q_evac"], 1)
                    dve.tensor_scalar(xq_t[:, :, :], SMALL[:, 0:2 * P].rearrange("p (c t) -> p c t", t=P), gxq[:, :], None,
                                      ALU.mult)
                    dve.tensor_copy(conv_in[:, :, 0:TAPS - 1], conv_in[:, :, P:P + TAPS - 1]).then_inc(s["halo"], 1)
                    have(dve, s["halo"], n - 1)
                    dve.tensor_copy(conv_in[:, :, TAPS - 1:], SMALL[:, 2 * P:4 * P].rearrange("p (h t) -> p h t", t=P)
                                    ).then_inc(s["xqc_evac"], 1)
                    have(dve, s["xqc_evac"], n - 1)
                    for j in range(TAPS):
                        if j:
                            have(dve, s["conv"], n - 1, TAPS, TAPS - j)
                        for h in range(LH):
                            tap = conv_in[:, h, j:j + P]
                            if j == 0:
                                last = dve.tensor_scalar(xc[:, h, :], tap, cw[:, h, 0:1], cb[:, h:h + 1], ALU.mult, ALU.add)
                            else:
                                last = dve.scalar_tensor_tensor(xc[:, h, :], tap, cw[:, h, j:j + 1], xc[:, h, :],
                                                                ALU.mult, ALU.add)
                        last.then_inc(s["conv"], 1)

                def head_sums(signal, done, at, heads):
                    have(dve, signal, n)
                    dve.tensor_reduce(ss[:, at:at + heads],
                                      squares[:, 0:heads * HD].rearrange("p (h d) -> p h d", d=HD), AX.X, ALU.add
                                      ).then_inc(done, 1)

                def stick(half):
                    have(dve, s[f"masked{half}"], n - 1)
                    flat = fail_g[:, half * HB * SEG:(half + 1) * HB * SEG][:, ::-1]
                    dve.tensor_tensor_scan(flat, flat, restart[:, ::-1], 1.0, ALU.mult, ALU.max
                                           ).then_inc(s[f"scan{half}"], 1)
                    have(dve, s[f"scan{half}"], n - 1)
                    hs = slice(half * HB, half * HB + HB)
                    if half == 0:
                        have_dma(dve, kept["carry"], n - 2)
                    dve.tensor_copy(carry[:, q, hs], fail[:, hs, 0])
                    dve.tensor_tensor(take[:, hs, :], take[:, hs, :], fail[:, hs, 1:SEG], ALU.mult
                                      ).then_inc(s[f"w{half}"], 1)

                def silu(signal, done, src, cols, group):
                    have(dve, signal, n)
                    dve.scalar_tensor_tensor(gate[:, p, cols], src, unscale[:, group:group + 1], gate[:, p, cols],
                                             ALU.mult, ALU.mult).then_inc(done, 1)

                if A:
                    head_sums(s["q_read"], s["q_sum"], 0, HS)
                if first:
                    next_chunk(2)
                    for m in range(MT):
                        memory_turned(m)
                if B:
                    stick(0)
                if A:
                    head_sums(s["k_read"], s["k_sum"], HS, HS)
                if first:
                    next_chunk(3)
                    memory_keys()
                    lru_start()
                    next_chunk(4)
                    chunk_factor(5)
                if B:
                    stick(1)
                    if isinstance(n, int) and n == 1:
                        dve.memset(left[:, :], 0.0).then_inc(s["left_done"], 1)
                    else:
                        have(dve, s["w1"], n - 1)
                        have(dve, s["left_done"], n - 2)
                        dve.tensor_tensor(left[:, :], left[:, :], carry[:, q, :], ALU.max).then_inc(s["left_done"], 1)
                if A:
                    head_sums(s["xa_read"], s["xq_sum"], 2 * HS, HX)
                    silu(s["xa_read"], s["gate_x"], PROJ[0][:, HX * HD:GC], slice(D - HX * HD, D), G_XA)
                if first:
                    chunk_low(5)
                    chunk_top(6)
                if B:
                    have(dve, s["xa_scores"], n - 1)
                    for odd in range(2):
                        last = dve.tensor_reduce(mx[:, odd::2], SCORE[odd][:, :].rearrange("p (h s) -> p h s", s=NM),
                                                 AX.X, ALU.max)
                    last.then_inc(s["mx_done"], 1)
                    have(dve, s["mx_done"], n - 1)
                    dve.tensor_scalar(neg_mx[:, :], mx[:, :], -ZSCALE, None, ALU.mult).then_inc(s["neg_done"], 1)
                if C:
                    have(dve, s["y_hi_done"], n - 2)
                    for b in range(2):
                        last = dve.tensor_tensor(y_lo[:, 4 * b:4 * b + 4, :], TURN[b][:, :].rearrange("p (k t) -> p k t", t=P),
                                                 y_hi[:, 4 * b:4 * b + 4, :], ALU.subtract)
                    last.then_inc(s["y_lo_done"], 1)
                if A:
                    have(dve, s["rs_done"], n)
                    for raw, at, heads in ((q_raw, 0, HS), (k_raw, HS, HS), (xq_raw, 2 * HS, HX)):
                        last = dve.tensor_tensor(raw[:, :, :], raw[:, :, :],
                                                 rs[:, at:at + heads].unsqueeze(2).to_broadcast([P, heads, HD]), ALU.mult)
                    last.then_inc(s["normed"], 1)
                if first:
                    memory_keys_norm()
                if B:
                    have(dve, s["tanh_done"], n - 1)
                    dve.tensor_scalar(beta[:, :, :], tanh_l[:, :, :], -1.0, 1.0, ALU.mult, ALU.add).then_inc(s["beta_steps"], 1)
                    have(dve, s["beta_steps"], n - 1, 3, 2)
                    dve.reciprocal(beta[:, :, :], beta[:, :, :]).then_inc(s["beta_steps"], 1)
                    have(dve, s["beta_steps"], n - 1, 3, 1)
                    flat = "p h t -> p (h t)"
                    dve.scalar_tensor_tensor(beta[:, :, :].rearrange(flat), tanh_l[:, :, :].rearrange(flat), -2.0,
                                             beta[:, :, :].rearrange(flat), ALU.mult, ALU.mult).then_inc(s["beta_steps"], 1)
                if first:
                    lru_rate()
                if A:
                    silu(s["lru_read"], s["gate_l"], PROJ[1][:, LW:GC], slice(D // 2, D // 2 + LW), G_LRU)
                if first:
                    chunk_factor(6)
                    chunk_low(6)
                    chunk_top(7)
                    memory_keys_turned()
                if B:
                    have(dve, s["w0_act"], n - 1)
                    turned_low(s["w0_dve"])
                if A:
                    silu(s["sg_read"], s["gate_sb"], PROJ[0][:, :], slice(0, GC), G_SG)
                if B:
                    have(dve, s["u_done"], n - 1)
                    for h in range(LH):
                        last = dve.tensor_tensor_scan(h_sb[:, h, :], decay[:, h, :], in_g[:, h, :],
                                                      h_sb[:, h, P - 1:P], ALU.mult, ALU.add)
                    last.then_inc(s["h_done"], 1)
                    have(dve, s["w1_act"], n - 1)
                    turned_low(s["w1_dve"])
                if X:
                    have(dve, s["x_rs"], n + 1)
                    dve.tensor_scalar(xy[:, :], xy[:, :], rs_x[:, :], None, ALU.mult).then_inc(s["x_scaled"], 1)
                    if isinstance(n, int) and n < 0:
                        chunk_top(0)
                if B:
                    have(dve, s["p_done"], n - 1)
                    dve.reciprocal(rden[:, :], den[:, :]).then_inc(s["rden_done"], 1)
                    have(dve, s["rden_done"], n - 1)
                    gx = gate[:, q, D - HX * HD:D].rearrange("p (h d) -> p h d", d=HD)
                    dve.tensor_tensor(gx, gx, rden[:, :].unsqueeze(2).to_broadcast([P, HX, HD]), ALU.mult
                                      ).then_inc(s["gx_done"], 1)
                if A:
                    have(dve, s["v_hi"], n)
                    dve.scalar_tensor_tensor(v_sb[:, p, 1, :], PROJ[1][:, :], VDOWN, v_sb[:, p, 0, :],
                                             ALU.mult, ALU.subtract).then_inc(s["v_read"], 1)
                if B:
                    have(dve, s["turned_p"], n - 1)
                    dve.tensor_copy(turned_f32[:, 4:8, :], TURN[1][:, :].rearrange("p (c t) -> p c t", t=P)
                                    ).then_inc(s["p_dve"], 1)
                if C:
                    have(dve, out_done[0], n - 2)
                    have_dma(dve, res_loaded, n - 2)
                    dve.scalar_tensor_tensor(x_res[:, 0:GC], PROJ[0][:, :], y_un[:, p, 0:1], x_res[:, 0:GC],
                                             ALU.mult, ALU.add).then_inc(s["out0_read"], 1)
                if B:
                    have(dve, s["mixed"], n - 1)
                    have(dve, s["gx_done"], n - 1)
                    if X:
                        have(dve, s["turned_x"], n + 1)
                    dve.scalar_tensor_tensor(xy[:, 0:GC], HEADS[:, :], unscale[:, G_V:G_V + 1], gate[:, q, 0:GC],
                                             ALU.mult, ALU.mult)
                    dve.tensor_tensor(xy[:, GC:GC + LW], SMALL[:, 2 * P:4 * P], gate[:, q, GC:GC + LW], ALU.mult)
                    dve.tensor_tensor(xy[:, GC + LW:D], SMALL[:, 0:HX * HD], gate[:, q, GC + LW:D], ALU.mult
                                      ).then_inc(s["y_mixed"], 1)
                if X:
                    have(dve, s["x_hi_done"], n + 1)
                    for b in range(2):
                        last = dve.tensor_tensor(x_lo[:, 4 * b:4 * b + 4, :], TURN[b][:, :].rearrange("p (k t) -> p k t", t=P),
                                                 x_hi[:, 4 * b:4 * b + 4, :], ALU.subtract)
                    last.then_inc(s["x_lo_done"], 1)
                if first:
                    chunk_factor(7)
                    chunk_low(7)
                if B:
                    have(dve, s["y_mixed"], n - 1)
                    dve.tensor_reduce(y_max[:, :], xy[:, :], AX.X, ALU.max, apply_absolute_value=True)\
                       .then_inc(s["y_steps"], 1)
                    have(dve, s["y_steps"], n - 1, 4, 3)
                    dve.tensor_scalar(y_max[:, :], y_max[:, :], 1e-30, None, ALU.max).then_inc(s["y_steps"], 1)
                    have(dve, s["y_steps"], n - 1, 4, 2)
                    dve.tensor_scalar(y_exp[:, :].bitcast(U32), y_max[:, :].bitcast(U32), EXPONENT, None, ALU.bitwise_and
                                      ).then_inc(s["y_steps"], 1)
                    have(dve, s["y_steps"], n - 1, 4, 1)
                    dve.tensor_scalar(y_un[:, q, :], unscale[:, 6:6 + OC], y_exp[:, :], 1.0 / TOP, ALU.mult, ALU.mult)
                    dve.reciprocal(y_inv[:, :], y_exp[:, :]).then_inc(s["y_steps"], 1)
                    have(dve, s["y_steps"], n - 1, 4)
                    dve.tensor_scalar(xy[:, :], xy[:, :], y_inv[:, :], TOP, ALU.mult, ALU.mult).then_inc(s["y_scaled"], 1)
                if C:
                    have(dve, out_done[1], n - 2)
                    dve.scalar_tensor_tensor(x_res[:, GC:D], PROJ[1][:, :], y_un[:, p, 1:2], x_res[:, GC:D],
                                             ALU.mult, ALU.add).then_inc(s["out_ready"], 1)

            steps(dve, body)

            dve.wait_ge(s["left_done"], NT)
            dve.tensor_reduce(left_max[:, :], left[:, :], AX.X, ALU.max).then_inc(left_top, 1)
            dve.wait_ge(left_top_all, 1)
            dve.tensor_scalar(go_on[:, :], left_all[:, :], 0.0, None, ALU.is_gt).then_inc(go_on_set, 1)

            def row(i, w, before, n_steps):
                have(dve, far_loaded, w, 64)
                dve.memset(xy[:, 0:GC], 0.0).then_inc(far_row["zero"], 1)
                have(dve, far_row["zero"], w, ahead_of_loop=True)
                with dve.Fori(0, n_steps) as j:
                    u = before + j
                    have(dve, far["sigmoids"], u)
                    dve.tensor_copy(fail[:, :, P], carry[:, 0, :]).then_inc(far["ends"], 1)
                    for h in range(HS):
                        flat = fail[:, h, 0:P][:, ::-1]
                        last = dve.tensor_tensor_scan(flat, flat, restart[:, 0:P], carry[:, 0, h:h + 1], ALU.mult, ALU.max)
                    last.then_inc(far["scanned"], 1)
                    have(dve, far["ends"], u)
                    have(dve, far["scanned"], u)
                    dve.tensor_copy(carry[:, 0, :], fail[:, :, 0])
                    dve.tensor_tensor(take[:, :, 0:P], take[:, :, 0:P], fail[:, :, 1:P + 1], ALU.mult
                                      ).then_inc(far["weights"], 1)
                    have(dve, far["t_act"], u)
                    turned_low(far["t_dve"])
                    have(dve, far["summed"], u)
                    dve.tensor_tensor(xy[:, 0:GC], xy[:, 0:GC], HEADS[:, :], ALU.add).then_inc(far["added"], 1)
                    have(dve, far["added"], u)
                dve.scalar_tensor_tensor(xy[:, 0:GC], xy[:, 0:GC], unscale[:, G_V:G_V + 1], gate[:, 0, 0:GC],
                                         ALU.mult, ALU.mult).then_inc(far_row["gated"], 1)
                have(dve, far_row["gated"], w)
                dve.tensor_reduce(y_max[:, :], xy[:, 0:GC], AX.X, ALU.max, apply_absolute_value=True).then_inc(far_row["steps"], 1)
                have(dve, far_row["steps"], w, 4, 3)
                dve.tensor_scalar(y_max[:, :], y_max[:, :], 1e-30, None, ALU.max).then_inc(far_row["steps"], 1)
                have(dve, far_row["steps"], w, 4, 2)
                dve.tensor_scalar(y_exp[:, :].bitcast(U32), y_max[:, :].bitcast(U32), EXPONENT, None, ALU.bitwise_and
                                  ).then_inc(far_row["steps"], 1)
                have(dve, far_row["steps"], w, 4, 1)
                dve.tensor_scalar(y_un[:, 0, :], unscale[:, 6:6 + OC], y_exp[:, :], 1.0 / TOP, ALU.mult, ALU.mult)
                dve.reciprocal(y_inv[:, :], y_exp[:, :]).then_inc(far_row["steps"], 1)
                have(dve, far_row["steps"], w, 4)
                dve.tensor_scalar(xy[:, 0:GC], xy[:, 0:GC], y_inv[:, :], TOP, ALU.mult, ALU.mult).then_inc(far_row["scaled"], 1)
                have(dve, far_row["hi"], w)
                dve.tensor_tensor(y_lo[:, 0:4, :], TURN[0][:, :].rearrange("p (k t) -> p k t", t=P), y_hi[:, 0:4, :],
                                  ALU.subtract).then_inc(far_row["lo"], 1)
                have(dve, far_row["products"], w)
                for c in range(OC):
                    part = x_res[:, c * GC:(c + 1) * GC]
                    last = dve.scalar_tensor_tensor(part, PROJ[c][:, :], y_un[:, 0, c:c + 1], part, ALU.mult, ALU.add)
                last.then_inc(far_row["result"], 1)

            rest(dve, row)

        @block.tensor
        def _(pe):
            pe.wait_ge(const_made, 1)

            def memory_product():
                for m in range(MT):
                    pe.wait_ge(m_scaled, m + 1)
                    if m:
                        pe.wait_ge(m_evac, m)
                    else:
                        have(pe, s["x_lo_done"], 0)
                    for k in range(KD):
                        last = pe.transpose(TURN[k // 4][:, (k % 4) * P:(k % 4 + 1) * P], mem_raw[:, m, k * P:(k + 1) * P],
                                            ident[:, :])
                    last.then_inc(m_turned, 1)
                pe.wait_ge(kv_loaded, 16)
                for m in range(MT):
                    pe.wait_ge(m_evac, m + 1)
                    for k in range(KD):
                        last = pe.matmul(SCORE[m][:, :], mem_t[:, k, m * P:(m + 1) * P], kv_raw[:, k, :],
                                         start=k == 0, stop=k == KD - 1)
                    last.then_inc(m_kv, 1)

            def memory_keys_turn():
                pe.wait_ge(m_kv_norm, 1)
                for c in range(MT * HX // 2):
                    last = pe.transpose(SMALL[:, c * P:(c + 1) * P], mk_raw[:, c * P:(c + 1) * P], ident[:, :])
                last.then_inc(m_k_turned, 1)

            def pair_product(dst, hi, lo, pair, done):
                for k in range(KD):
                    pe.matmul(dst, hi[:, k, :], pair[:, 0, k, :], start=k == 0, stop=False)
                    pe.matmul(dst, hi[:, k, :], pair[:, 1, k, :], start=False, stop=False)
                    last = pe.matmul(dst, lo[:, k, :], pair[:, 0, k, :], start=False, stop=k == KD - 1)
                last.then_inc(done, 1)

            def body(n, p):
                X, A, B, C = stages(n)
                q = 1 - p
                static = isinstance(n, int)

                def project(c, free):
                    if not A:
                        return
                    if static and n == 0:
                        pe.wait_ge(w_lo, c + 1)
                    for signal, tile in free:
                        have(pe, signal, tile)
                    pair_product(PROJ[c % 2][:, :], x_hi, x_lo, w_pair[:, ORDER[c]], proj_done[c])

                def turn(src, dst):
                    pe.transpose(dst, src, ident[:, :])

                if A:
                    have(pe, s["x_hi_done"], n)
                    have(pe, s["x_lo_done"], n)
                if B:
                    have(pe, s["normed"], n - 1)
                    have(pe, s["lru_read"], n - 1)
                    have(pe, s["y_mixed"], n - 2)
                    have(pe, s["p_act"], n - 2)
                    have(pe, s["p_dve"], n - 2)
                    for c in range(4):
                        turn(q_raw[:, 2 * c:2 * c + 2, :].rearrange("p h d -> p (h d)"), TURN[0][:, c * P:(c + 1) * P])
                    for c in range(4):
                        turn(k_raw[:, 2 * c:2 * c + 2, :].rearrange("p h d -> p (h d)"), TURN[1][:, c * P:(c + 1) * P])
                    for c in range(2):
                        turn(xq_raw[:, 2 * c:2 * c + 2, :].rearrange("p h d -> p (h d)"), SMALL[:, c * P:(c + 1) * P])
                    for c in range(LH):
                        pe_last = pe.transpose(SMALL[:, (2 + c) * P:(3 + c) * P], lx_raw[:, c * P:(c + 1) * P], ident[:, :])
                    pe_last.then_inc(s["turned_qk"], 1)
                project(0, [(s["gate_sb"], n - 1)])

                def scores(half):
                    for h in range(half * HB, half * HB + HB):
                        r = slice((h % 2) * HD, (h % 2 + 1) * HD)
                        at = ((h // 2) % 2) * HW
                        z = SCORE[h % 2]
                        pe.matmul(z[:, at:at + P], q_t[r, h // 2, :], k_t[r, p, h // 2, :], start=True, stop=True)
                        last = pe.matmul(z[:, at + P:at + HW], q_t[r, h // 2, :], k_t[r, q, h // 2, :], start=True, stop=True)
                    last.then_inc(s[f"scores{half}"], 1)

                if B:
                    have(pe, s["q_evac"], n - 1)
                    have(pe, s["k_evac"], n - 1)
                    have(pe, s["p_done"], n - 2)
                    scores(0)
                project(1, [(s["v_read"], n - 1)])
                if B:
                    have(pe, s["sig0"], n - 1)
                    scores(1)
                if static and n == 0:
                    memory_product()
                project(2, [(s["q_read"], n)])
                if B:
                    have(pe, s["sig1"], n - 1)
                    have(pe, s["xqc_evac"], n - 1)
                    if static and n == 1:
                        pe.wait_ge(m_done, 1)
                    for h in range(HX):
                        r = slice((h % 2) * HD, (h % 2 + 1) * HD)
                        last = pe.matmul(SCORE[h % 2][:, (h // 2) * NM:(h // 2 + 1) * NM], xq_t[r, h // 2, :],
                                         mk_t[r, h // 2, :], start=True, stop=True)
                    last.then_inc(s["xa_scores"], 1)
                    have(pe, s["conv"], n - 1, TAPS)
                    for g, blocks in enumerate((rg_blocks, ig_blocks)):
                        for h in range(LH):
                            at = (g * LH + h) * P
                            last = pe.matmul(SMALL[:, at:at + P], blocks[:, h, :], xc[:, h, :], start=True, stop=True)
                    last.then_inc(s["gates_done"], 1)
                if C:
                    have(pe, s["y_scaled"], n - 2)
                    if B:
                        have(pe, s["q_evac"], n - 1)
                        have(pe, s["k_evac"], n - 1)
                    else:
                        have(pe, s["p_act"], n - 2)
                        have(pe, s["p_dve"], n - 2)
                    for k in range(KD):
                        last = pe.transpose(TURN[k // 4][:, (k % 4) * P:(k % 4 + 1) * P], xy[:, k * P:(k + 1) * P], ident[:, :])
                    last.then_inc(s["turned_y"], 1)
                project(3, [(s["k_read"], n)])
                def turn_weights(src, signal):
                    for i in range(8):
                        last = pe.transpose(TURN[i // 4][:, (i % 4) * P:(i % 4 + 1) * P],
                                            src[:, i // 2, (i % 2) * P:(i % 2 + 1) * P], ident[:, :])
                    last.then_inc(signal, 1)

                def weigh(half_heads, signal):
                    for i in range(4):
                        cols = slice((half_heads * 4 + i) * HD, (half_heads * 4 + i + 1) * HD)
                        for own in range(2):
                            hi, lo = turned[:, 0, 2 * i + own, :], turned[:, 1, 2 * i + own, :]
                            v = v_sb[:, q if own else p, :, cols]
                            pe.matmul(HEADS[:, cols], hi, v[:, 0, :], start=own == 0, stop=False)
                            pe.matmul(HEADS[:, cols], hi, v[:, 1, :], start=False, stop=False)
                            last = pe.matmul(HEADS[:, cols], lo, v[:, 0, :], start=False, stop=own == 1)
                    last.then_inc(signal, 1)

                if B:
                    have(pe, s["w0"], n - 1)
                    if C:
                        have(pe, s["y_lo_done"], n - 2)
                    turn_weights(take[:, 0:4, :], s["turned_w0"])
                project(4, [(s["gate_x"], n)])
                if static and n == 0:
                    memory_keys_turn()
                if B:
                    have(pe, s["w0_act"], n - 1)
                    have(pe, s["w0_dve"], n - 1)
                    have(pe, s["v_read"], n - 1)
                    weigh(0, s["heads0"])
                    have(pe, s["w1"], n - 1)
                    turn_weights(take[:, 4:8, :], s["turned_w1"])
                project(5, [(s["gate_l"], n)])
                if B:
                    have(pe, s["w1_act"], n - 1)
                    have(pe, s["w1_dve"], n - 1)
                    weigh(1, s["heads1"])
                    have(pe, s["p_done"], n - 1)
                    turn_weights(probs, s["turned_p"])
                if C:
                    have(pe, s["y_hi_done"], n - 2)
                    have(pe, s["y_lo_done"], n - 2)
                    if A:
                        have(pe, s["gate_sb"], n)
                    pair_product(PROJ[0][:, :], y_hi, y_lo, wo_pair[:, 0], out_done[0])
                if B:
                    have(pe, s["p_act"], n - 1)
                    have(pe, s["p_dve"], n - 1)
                    have(pe, s["gates_read"], n - 1)
                    for h in range(HX):
                        for m in range(MT):
                            pe.matmul(SMALL[:, h * HD:(h + 1) * HD], turned_f32[:, MT * h + m, :],
                                      mv_sb[:, m, h * HD:(h + 1) * HD], start=m == 0, stop=m == MT - 1)
                    have(pe, s["h_done"], n - 1)
                    for h in range(LH):
                        last = pe.transpose(SMALL[:, (2 + h) * P:(3 + h) * P], h_sb[:, h, :], ident[:, :])
                    last.then_inc(s["mixed"], 1)
                if X:
                    have(pe, s["x_scaled"], n + 1)
                    if A and not B:
                        have(pe, s["x_lo_done"], n)
                    for k in range(KD):
                        last = pe.transpose(TURN[k // 4][:, (k % 4) * P:(k % 4 + 1) * P], xy[:, k * P:(k + 1) * P], ident[:, :])
                    last.then_inc(s["turned_x"], 1)
                if C:
                    if A:
                        have(pe, s["v_read"], n)
                    pair_product(PROJ[1][:, :], y_hi, y_lo, wo_pair[:, 1], out_done[1])

            steps(pe, body)

            def row(i, w, before, n_steps):
                have(pe, far_loaded, w, 64, ahead_of_loop=True)
                with pe.Fori(0, n_steps) as j:
                    u = before + j
                    have(pe, far_kv, u, 32)
                    for h in range(HS):
                        r = slice((h % 2) * HD, (h % 2 + 1) * HD)
                        last = pe.matmul(SCORE[h % 2][:, (h // 2) * P:(h // 2 + 1) * P], q_t[r, h // 2, :],
                                         k_t[r, 0, h // 2, :], start=True, stop=True)
                    last.then_inc(far["scored"], 1)
                    have(pe, far["weights"], u)
                    for h in range(HS):
                        last = pe.transpose(TURN[h // 4][:, (h % 4) * P:(h % 4 + 1) * P], take[:, h, 0:P], ident[:, :])
                    last.then_inc(far["turned"], 1)
                    have(pe, far["t_act"], u)
                    have(pe, far["t_dve"], u)
                    for h in range(HS):
                        cols = slice(h * HD, (h + 1) * HD)
                        pe.matmul(HEADS[:, cols], turned[:, 0, h, :], v_sb[:, 0, 0, cols], start=True, stop=False)
                        pe.matmul(HEADS[:, cols], turned[:, 0, h, :], v_sb[:, 0, 1, cols], start=False, stop=False)
                        last = pe.matmul(HEADS[:, cols], turned[:, 1, h, :], v_sb[:, 0, 0, cols], start=False, stop=True)
                    last.then_inc(far["summed"], 1)
                    have(pe, far["added"], u)
                have(pe, far_row["scaled"], w)
                for k in range(4):
                    last = pe.transpose(TURN[0][:, k * P:(k + 1) * P], xy[:, k * P:(k + 1) * P], ident[:, :])
                last.then_inc(far_row["turned_y"], 1)
                have(pe, far_row["lo"], w)
                for c in range(OC):
                    for k in range(4):
                        pe.matmul(PROJ[c][:, :], y_hi[:, k, :], wo_pair[:, c, 0, k, :], start=k == 0, stop=False)
                        pe.matmul(PROJ[c][:, :], y_hi[:, k, :], wo_pair[:, c, 1, k, :], start=False, stop=False)
                        last = pe.matmul(PROJ[c][:, :], y_lo[:, k, :], wo_pair[:, c, 0, k, :], start=False, stop=k == 3)
                last.then_inc(far_row["products"], 1)
                have(pe, far_row["result"], w)

            rest(pe, row)


_INS = ["x", "mem", "norm_g", "w_in", "sb_q_g", "sb_k_g", "conv_w", "conv_b", "w_rg", "b_rg", "w_ig", "b_ig",
        "lru_lambda", "xa_q_g", "xa_k_g", "mem_g", "w_mem_kv", "w_out"]


def kernel(**inputs):
    import concourse.bacc as bacc
    from concourse.bass_utils import run_bass_kernel_spmd

    nc = bacc.Bacc("TRN2", target_bir_lowering=False, num_devices=1)
    arrays, args = {}, []
    for name in _INS:
        a = np.ascontiguousarray(inputs[name])
        arrays[f"in_{name}"] = a
        args.append(nc.dram_tensor(f"in_{name}", a.shape, mybir.dt.from_np(a.dtype), kind="ExternalInput").ap())
    shape = inputs["x"].shape
    args.append(nc.dram_tensor("out_0", shape, F32, kind="ExternalOutput").ap())
    hybrid_layer(nc, *args)
    r = run_bass_kernel_spmd(nc, [arrays], core_ids=[0])
    return r.results[0]["out_0"]
```
